# Optimizing a Trainium2 kernel written in Bass

```python
import jax, jax.numpy as jnp
from jax import lax
import numpy as np

D_MODEL = 1024
BATCH = 1
SEQ = 512
DEPTH = 2

CHUNK = 64
RET_HEADS = 4
RET_HEAD_DIM = 128
RET_WIDTH = RET_HEADS * RET_HEAD_DIM
RWKV_HEADS = 8
RWKV_HEAD_DIM = 64
RWKV_WIDTH = RWKV_HEADS * RWKV_HEAD_DIM
DECAY_LORA = 64
AAA_LORA = 64
MV_LORA = 32
GATE_LORA = 160
D_FF = 2816
CONV_WIDTH = 3
ROPE_BASE = 10000.0
LN_EPS = 1e-5
RET_NORM_EPS = 1e-6
LNX_EPS = 64e-5
DEEPNORM_ALPHA = (2 * DEPTH) ** 0.25
DEEPNORM_BETA = (8 * DEPTH) ** -0.25
RWKV_SHIFT_WIDTH = 3 * RWKV_WIDTH + DECAY_LORA + AAA_LORA + GATE_LORA
IN_WIDTH = 4 * RET_WIDTH + RWKV_SHIFT_WIDTH + 2 * D_MODEL

kernel_name = 'hybrid_retention_rwkv7_deepnorm'

def _split(t, sizes):
    out, o = [], 0
    for s in sizes:
        out.append(t[..., o:o + s])
        o += s
    return out

def _layer_norm(x, g, b):
    xf = x.astype(jnp.float32)
    xc = xf - jnp.mean(xf, -1, keepdims=True)
    var = jnp.mean(xc * xc, -1, keepdims=True)
    return xc * lax.rsqrt(var + LN_EPS) * g.astype(jnp.float32) + b.astype(jnp.float32)

def _token_shift(z, mu):
    z_prev = jnp.pad(z[:, :-1], ((0, 0), (1, 0), (0, 0)))
    return z + mu * (z_prev - z)

def _rotary(t, pos):
    half = t.shape[-1] // 2
    inv_freq = ROPE_BASE ** (-jnp.arange(half, dtype=jnp.float32) / half)
    ang = pos[:, None] * inv_freq[None, :]
    cos = jnp.cos(ang)[None, :, None, :]
    sin = jnp.sin(ang)[None, :, None, :]
    t1, t2 = t[..., :half], t[..., half:]
    return jnp.concatenate([t1 * cos - t2 * sin, t1 * sin + t2 * cos], -1)

def _retention_core(q, k, v):
    B, S, H, Dh = q.shape
    N = S // CHUNK
    log_g = jnp.log(1.0 - 2.0 ** (-5.0 - jnp.arange(H, dtype=jnp.float32)))
    idx = jnp.arange(CHUNK, dtype=jnp.float32)
    intra_decay = jnp.exp(log_g[:, None, None] * jnp.abs(idx[:, None] - idx[None, :]))
    q_decay = jnp.exp(log_g[None, :] * (idx[:, None] + 1.0))
    k_decay = jnp.exp(log_g[None, :] * (CHUNK - 1.0 - idx[:, None]))
    chunk_decay = jnp.exp(log_g * CHUNK)
    qc = q.reshape(B, N, CHUNK, H, Dh)
    kc = k.reshape(B, N, CHUNK, H, Dh)
    vc = v.reshape(B, N, CHUNK, H, Dh)
    scores = jnp.einsum('bnchd,bnshd->bnhcs', qc, kc) * intra_decay
    intra = jnp.einsum('bnhcs,bnshd->bnchd', scores, vc)

    def step(R, inp):
        qi, ki, vi = inp
        cross = jnp.einsum('bchd,bhde->bche', qi, R) * q_decay[None, :, :, None]
        R = R * chunk_decay[None, :, None, None] + jnp.einsum(
            'bchd,bche->bhde', ki * k_decay[None, :, :, None], vi)
        return R, cross

    R0 = jnp.zeros((B, H, Dh, Dh), jnp.float32)
    xs = (jnp.moveaxis(qc, 1, 0), jnp.moveaxis(kc, 1, 0), jnp.moveaxis(vc, 1, 0))
    _, cross = lax.scan(step, R0, xs)
    cross = jnp.moveaxis(cross, 0, 1)
    return (intra + cross).reshape(B, S, H, Dh)

def _retention_branch(q, k, v, g, pos, w_o):
    B, S, _ = q.shape
    shp = (B, S, RET_HEADS, RET_HEAD_DIM)
    qh = _rotary(q.astype(jnp.float32).reshape(shp), pos)
    kh = _rotary(k.astype(jnp.float32).reshape(shp), pos) * RET_HEAD_DIM ** -0.5
    vh = v.astype(jnp.float32).reshape(shp)
    o = _retention_core(qh, kh, vh)
    o = o * lax.rsqrt(jnp.mean(o * o, -1, keepdims=True) + RET_NORM_EPS)
    o = o.reshape(B, S, RET_WIDTH) * jax.nn.silu(g.astype(jnp.float32))
    return o.astype(q.dtype) @ w_o

def _rwkv7_recurrence(r, w, k, v, a, b):
    B, S, H, N = r.shape

    def step(state, inp):
        r_t, w_t, k_t, v_t, a_t, b_t = inp
        sa = jnp.einsum('bhij,bhj->bhi', state, a_t)
        state = (state * w_t[:, :, None, :] + sa[..., None] * b_t[:, :, None, :]
                 + v_t[..., None] * k_t[:, :, None, :])
        y = jnp.einsum('bhij,bhj->bhi', state, r_t)
        return state, y

    xs = tuple(jnp.moveaxis(t, 1, 0) for t in (r, w, k, v, a, b))
    _, y = lax.scan(step, jnp.zeros((B, H, N, N), jnp.float32), xs)
    return jnp.moveaxis(y, 0, 1)

def _rwkv7_branch(z, v_first, vres, w0, w2, a0, a2, g2, k_k, k_a, r_k, lnx_g, lnx_b, w_o):
    B, S, _ = z.shape
    f32 = jnp.float32
    r, k, v, wl, al, gl = _split(z, [RWKV_WIDTH] * 3 + [DECAY_LORA, AAA_LORA, GATE_LORA])
    w_log = -jax.nn.softplus(-(w0 + jnp.tanh(wl) @ w2)) - 0.5
    decay = jnp.exp(-jnp.exp(w_log.astype(f32)))
    a = jax.nn.sigmoid(a0 + al @ a2)
    if vres is None:
        v_first = v
    else:
        vl, v0, v2 = vres
        v = v + (v_first - v) * jax.nn.sigmoid(v0 + vl @ v2)
    g = jax.nn.sigmoid(gl) @ g2

    def heads(t):
        return t.astype(f32).reshape(B, S, RWKV_HEADS, RWKV_HEAD_DIM)

    kk = heads(k * k_k)
    kk = kk / jnp.maximum(jnp.sqrt(jnp.sum(kk * kk, -1, keepdims=True)), 1e-12)
    k = k * (1.0 + (a - 1.0) * k_a)
    rh, kh, vh, ah = heads(r), heads(k), heads(v), heads(a)
    y = _rwkv7_recurrence(rh, heads(decay), kh, vh, -kk, kk * ah)
    yc = y - jnp.mean(y, -1, keepdims=True)
    yn = yc * lax.rsqrt(jnp.mean(yc * yc, -1, keepdims=True) + LNX_EPS)
    yn = yn.reshape(B, S, RWKV_WIDTH) * lnx_g + lnx_b
    bonus = jnp.sum(rh * kh * r_k, -1, keepdims=True) * vh
    y = yn + bonus.reshape(B, S, RWKV_WIDTH)
    return (y * g).astype(z.dtype) @ w_o, v_first

def _causal_dwconv(z, w, b):
    S = z.shape[1]
    zp = jnp.pad(z, ((0, 0), (CONV_WIDTH - 1, 0), (0, 0)))
    out = zp[:, 0:S] * w[0]
    for j in range(1, CONV_WIDTH):
        out = out + zp[:, j:j + S] * w[j]
    return out + b

def setup_inputs(seed: int = 0) -> dict:
    key = jax.random.key(seed)
    ks = iter(jax.random.split(key, 40))
    f32 = jnp.float32
    L, D = DEPTH, D_MODEL
    beta = DEEPNORM_BETA

    def nrm(shape, scale):
        return jax.random.normal(next(ks), shape, f32) * scale

    x = nrm((BATCH, SEQ, D), 1.0)
    col_scale = np.ones((IN_WIDTH,), np.float32)
    col_scale[2 * RET_WIDTH:3 * RET_WIDTH] = beta
    rv = 4 * RET_WIDTH + 2 * RWKV_WIDTH
    col_scale[rv:rv + RWKV_WIDTH] = beta
    w_in = nrm((L, D, IN_WIDTH), D ** -0.5) * jnp.asarray(col_scale)
    mu_shift = jax.random.uniform(next(ks), (L, RWKV_SHIFT_WIDTH), f32)
    w_vres_in = nrm((L - 1, D, MV_LORA), D ** -0.5)
    mu_vres = jax.random.uniform(next(ks), (L - 1, MV_LORA), f32)
    v0 = 1.0 + nrm((L - 1, RWKV_WIDTH), 0.1)
    v2 = nrm((L - 1, MV_LORA, RWKV_WIDTH), MV_LORA ** -0.5)
    w0 = jax.random.uniform(next(ks), (L, RWKV_WIDTH), f32, -3.0, 0.0)
    w2 = nrm((L, DECAY_LORA, RWKV_WIDTH), 0.5 * DECAY_LORA ** -0.5)
    a0 = nrm((L, RWKV_WIDTH), 0.1)
    a2 = nrm((L, AAA_LORA, RWKV_WIDTH), AAA_LORA ** -0.5)
    g2 = nrm((L, GATE_LORA, RWKV_WIDTH), GATE_LORA ** -0.5)
    k_k = 0.85 + nrm((L, RWKV_WIDTH), 0.05)
    k_a = 1.0 + nrm((L, RWKV_WIDTH), 0.05)
    r_k = nrm((L, RWKV_HEADS, RWKV_HEAD_DIM), 0.1)
    lnx_g = 1.0 + nrm((L, RWKV_WIDTH), 0.05)
    lnx_b = nrm((L, RWKV_WIDTH), 0.02)
    w_ret_o = nrm((L, RET_WIDTH, D), RET_WIDTH ** -0.5 * beta)
    w_rwkv_o = nrm((L, RWKV_WIDTH, D), RWKV_WIDTH ** -0.5 * beta)
    w_out = nrm((L, D, D), D ** -0.5 * beta)
    ln1_g = 1.0 + nrm((L, D), 0.05)
    ln1_b = nrm((L, D), 0.02)
    w_up = nrm((L, D, 2 * D_FF), D ** -0.5)
    conv_w = nrm((L, CONV_WIDTH, D_FF), CONV_WIDTH ** -0.5)
    conv_b = nrm((L, D_FF), 0.02)
    w_down = nrm((L, D_FF, D), D_FF ** -0.5 * beta)
    ln2_g = 1.0 + nrm((L, D), 0.05)
    ln2_b = nrm((L, D), 0.02)
    return {'x': x, 'w_in': w_in, 'mu_shift': mu_shift, 'w_vres_in': w_vres_in,
            'mu_vres': mu_vres, 'v0': v0, 'v2': v2, 'w0': w0, 'w2': w2, 'a0': a0,
            'a2': a2, 'g2': g2, 'k_k': k_k, 'k_a': k_a, 'r_k': r_k, 'lnx_g': lnx_g,
            'lnx_b': lnx_b, 'w_ret_o': w_ret_o, 'w_rwkv_o': w_rwkv_o, 'w_out': w_out,
            'ln1_g': ln1_g, 'ln1_b': ln1_b, 'w_up': w_up, 'conv_w': conv_w,
            'conv_b': conv_b, 'w_down': w_down, 'ln2_g': ln2_g, 'ln2_b': ln2_b}

def reference(x, w_in, mu_shift, w_vres_in, mu_vres, v0, v2, w0, w2, a0, a2, g2, k_k, k_a,
              r_k, lnx_g, lnx_b, w_ret_o, w_rwkv_o, w_out, ln1_g, ln1_b, w_up, conv_w,
              conv_b, w_down, ln2_g, ln2_b):
    dtype = x.dtype
    S = x.shape[1]
    pos = jnp.arange(S, dtype=jnp.float32)
    v_first = None
    for l in range(DEPTH):
        if l == 0:
            h = x @ w_in[0]
            vres_in = None
        else:
            h = x @ jnp.concatenate([w_in[l], w_vres_in[l - 1]], axis=1)
        q, k, v, g_ret, rw, gate_a, gate_b = _split(
            h, [RET_WIDTH] * 4 + [RWKV_SHIFT_WIDTH, D_MODEL, D_MODEL])
        if l > 0:
            vl = _token_shift(h[..., IN_WIDTH:], mu_vres[l - 1])
            vres_in = (vl, v0[l - 1], v2[l - 1])
        ret_out = _retention_branch(q, k, v, g_ret, pos, w_ret_o[l])
        rwkv_out, v_first = _rwkv7_branch(
            _token_shift(rw, mu_shift[l]), v_first, vres_in, w0[l], w2[l], a0[l], a2[l],
            g2[l], k_k[l], k_a[l], r_k[l], lnx_g[l], lnx_b[l], w_rwkv_o[l])
        mixed = jax.nn.sigmoid(gate_a) * ret_out + jax.nn.sigmoid(gate_b) * rwkv_out
        x = _layer_norm(DEEPNORM_ALPHA * x + mixed @ w_out[l], ln1_g[l], ln1_b[l]).astype(dtype)
        up = x @ w_up[l]
        gate = _causal_dwconv(up[..., :D_FF], conv_w[l], conv_b[l])
        ffn = (jax.nn.silu(gate) * up[..., D_FF:]) @ w_down[l]
        x = _layer_norm(DEEPNORM_ALPHA * x + ffn, ln2_g[l], ln2_b[l]).astype(dtype)
    return x


_drawn_inputs = setup_inputs


def setup_inputs(seed=0):
    import zlib

    import numpy as np

    out = dict(_drawn_inputs(seed))
    spreads = {}
    factors = {'w_vres_in': 4.002,
     'mu_vres': 8.0,
     'v0': 33.599,
     'v2': 3.998,
     'w2': 8.0,
     'a0': 8.0,
     'k_k': 37.069,
     'k_a': 8.0,
     'r_k': 7.391,
     'lnx_g': 8.0,
     'lnx_b': 32.353,
     'conv_b': 8.0}
    for name, (base, spread) in spreads.items():
        noise = np.random.default_rng([zlib.crc32(name.encode()), seed]).standard_normal(out[name].shape)
        drawn = base * np.exp(spread * noise) if base else spread * noise
        out[name] = __import__('jax').numpy.asarray(drawn.astype(out[name].dtype))
    for name, factor in factors.items():
        out[name] = (out[name] * factor).astype(out[name].dtype)
    return out
```

```python
from contextlib import ExitStack

import concourse.bass as bass
from concourse import mybir

F32 = mybir.dt.float32
F32R = mybir.dt.float32r
ACT = mybir.ActivationFunctionType
ALU = mybir.AluOpType

P = 128
LAYERS = 2
D = 1024
T = 512
KT = D // P
CH = 64
NCH = T // CH
RH = 4
RW_TILES = 4
FF = 2816
FT = FF // P
RING = 3
ALPHA = (2 * LAYERS) ** 0.25
LN_EPS, RET_EPS, LNX_EPS = 1e-5, 1e-6, 64e-5
LOG_DECAY = 0.6065306597126334

U_RET, U_RETV, U_LORA, U_RKV, U_GA, U_GB, U_OUT, U_UP, U_DOWN = 0, 12, 16, 19, 31, 43, 55, 63, 107
UNITS = 129
ALL_UNITS = LAYERS * UNITS

C_MU, C_W0, C_A0, C_V0, C_KK, C_KA, C_RK, C_LXG, C_LXB = 0, 15, 19, 23, 27, 31, 35, 39, 43
C_L1G, C_L1B, C_L2G, C_L2B, C_CW, C_CB, C_SEL = 47, 55, 63, 71, 79, 145, 167
C_LW, C_LG, C_LG2, C_LV = 168, 680, 1192, 1704
NPAR = 2216
K_ID, K_ONE, K_BLK, K_MASK, K_LEV, K_SCAN, K_EPS = 0, 128, 256, 384, 512, 896, 1408
NCONST = 1416


class Count:

    def __init__(self, sem, per_layer, credit=0):
        self.sem, self.per_layer, self.credit = sem, per_layer, credit
        self.base, self.k = credit, 0

    def layer(self, l):
        self.base, self.k = l * self.per_layer + self.credit, 0

    def inc(self, instruction):
        instruction.then_inc(self.sem, 1)
        self.k += 1

    def enter(self, i, each):
        self.saved, self.each = (self.base, self.k), each
        self.base = self.base + self.k + i * each
        self.k = 0

    def leave(self, turns):
        assert self.k == self.each, (self.sem, self.k, self.each)
        self.base, self.k = self.saved[0], self.saved[1] + self.each * turns

    def end(self):
        assert self.k == self.per_layer, (self.sem, self.k, self.per_layer)

    @property
    def now(self):
        return self.base + self.k


def build(nc, x_d, w_d, par_d, const_d, tab_d, out_d):
    with ExitStack() as ctx:
        base = 16512

        def at(name, shape, dt, offset):
            return nc.alloc_sbuf_tensor_at(name, shape, dt, offset=base + offset)

        KB = 1024
        raw = [at(f"raw{s}", [P, 8 * P], F32, s * 4 * KB) for s in range(RING)]
        hi = [at(f"hi{s}", [P, 8 * P], F32R, (12 + s * 4) * KB) for s in range(RING)]
        lo = [at(f"lo{s}", [P, 8 * P], F32R, (24 + s * 4) * KB) for s in range(RING)]
        xh = at("xh", [P, KT, T], F32R, 36 * KB)
        xl = at("xl", [P, KT, T], F32R, 52 * KB)
        o = 68 * KB
        cst = at("cst", [P, NCONST], F32, o)
        o += NCONST * 4
        par = at("par", [P, NPAR], F32, o)
        o += NPAR * 4
        tab = [at(f"tab{i}", [P, T], F32, o + i * 2 * KB) for i in range(2)]
        o += 4 * KB
        o = (o + 31) // 32 * 32
        R = o
        x_sum = at("x_sum", [P, KT, T], F32, R)
        qk = at("qk", [P, 2 * RH, T], F32, R)
        o_ret = qk
        oh = at("oh", [P, RH, T], F32R, R + 24 * KB)
        gs = at("gs", [P, RH, T], F32, R + 16 * KB)
        ol = at("ol", [P, RH, T], F32R, R + 16 * KB)
        vn = at("vn", [P, 4, T], F32, R + 24 * KB)
        ma = at("ma", [P, KT, T], F32, R)
        q = R + 32 * KB
        zr = at("zr", [P, 4, T + 1], F32, q)
        zk = at("zk", [P, 4, T + 1], F32, q + 8224)
        zv = at("zv", [P, 4, CH + T], F32, q + 16448)
        zl = at("zl", [P, 3, T + 1], F32, q + 25664)
        q += 31840
        ka_ = at("ka_", [P, 4, T], F32, q)
        kn = at("kn", [P, 4, T], F32, q + 8 * KB)
        pd = at("pd", [P, 4, NCH * (CH + 1)], F32, q + 16 * KB)
        pi = at("pi", [P, 4, T], F32, q + 16 * KB + 8320)
        bon = at("bon", [P, 4, T], F32, q + 24 * KB + 8320)
        q += 32 * KB + 8320
        pc = at("pc", [P, NCH, 4], F32, q)
        nka = at("nka", [P, 4], F32, q + 128)
        q += 160
        q = max(q, R + 104 * KB)
        tmp = [at(f"tmp{i}", [P, T], F32, q + i * 2 * KB) for i in range(4)]
        q += 8 * KB
        v_first = at("v_first", [P, 4, T], F32, q)
        q += 8 * KB
        assert base + q <= 229344, q
        c0 = R + 16 * KB
        arc = [at(f"arc{b}", [P, 4, 2, CH], F32, c0 + b * 2 * KB) for b in range(2)]
        bkc = at("bkc", [P, 4, 2, CH], F32, c0 + 4 * KB)
        am = [at(f"am{b}", [P, 2, 4, P], F32, c0 + (6 + 4 * b) * KB) for b in range(2)]
        vc = at("vc", [P, 4, P], F32, c0 + 14 * KB)
        c1 = R + 32 * KB + 31840 + 16 * KB
        vz = [at(f"vz{b}", [P, T], F32, c1 + b * 2 * KB) for b in range(2)]
        bkn = [at(f"bkn{b}", [P, T], F32, c1 + (4 + 2 * b) * KB) for b in range(2)]
        xt = [at(f"xt{b}", [CH, T], F32, c1 + (8 + 2 * b) * KB) for b in range(2)]
        xx = at("xx", [CH, T], F32, c1 + 12 * KB)
        z1 = at("z1", [CH, T], F32, c1 + 14 * KB)
        uv = tmp[0]
        ltm, rhs = tmp[1], tmp[2]
        hbd = at("hbd", [P, 4, P], F32, q - 10 * KB)
        hc = at("hc", [P, 4, CH], F32, R + 32 * KB + 25664)
        ht = at("ht", [P, 4, CH], F32, R + 32 * KB + 25664 + KB)
        yh = at("yh", [P, 4, T], F32R, R + 16 * KB)
        yl = at("yl", [P, 4, T], F32R, R + 24 * KB)
        b0 = R + 32 * KB + 31840
        mh = at("mh", [P, KT, T], F32R, b0)
        ml = at("ml", [P, KT, T], F32R, b0 + 16 * KB)
        gb = at("gb", [P, KT, T], F32, b0 + 16 * KB)
        ah = at("ah", [P, FT, T], F32R, R + 16 * KB)
        al = at("al", [P, FT, T], F32R, R + 60 * KB)
        assert 16 * KB + 88 * KB <= q - 8 * KB - R
        cg = [at("cg", [P, T + 2], F32, R)]
        cc = [at("cc", [P, T], F32, R + 4160)]
        sg = at("sg", [P, T], F32, R + 4160 + 4 * KB)
        fa = at("fa", [P, T], F32, R + 4160 + 6 * KB)

        ps = ctx.enter_context(nc.psum_tensor("ps", [P, 8, 512], F32))

        def sem(name):
            return ctx.enter_context(nc.semaphore(name))

        raw_loaded = [sem(f"raw_loaded{s}") for s in range(RING)]
        hi_ready, lo_ready, unit_done = sem("hi_ready"), sem("lo_ready"), sem("unit_done")
        const_loaded, par_loaded = sem("const_loaded"), sem("par_loaded")
        x_loaded = [sem(f"x_loaded{i}") for i in range(2)]
        tab_loaded = [sem(f"tab_loaded{i}") for i in range(2)]
        x_hi, x_split = sem("x_hi"), sem("x_split")
        rot_swapped, ret_in, ret_evac = sem("rot_swapped"), sem("ret_in"), sem("ret_evac")
        v_nat = sem("v_nat")
        z_evac, z_shifted = sem("z_evac"), sem("z_shifted")
        lora_act, lora_done, lora_evac = sem("lora_act"), sem("lora_done"), sem("lora_evac")
        dve = sem("dve_step")
        kk_raw, kk_sq, kk_sum, kk_root = sem("kk_raw"), sem("kk_sq"), sem("kk_sum"), sem("kk_root")
        scanned, decay_done = sem("scanned"), sem("decay_done")
        v_mixed = sem("v_mixed")
        bon_in, bon_sum, bon_done = sem("bon_in"), sem("bon_sum"), sem("bon_done")
        st_done, sc_ready, o_acc = sem("st_done"), sem("sc_ready"), sem("o_acc")
        o_sq, o_sum, o_root, o_norm, o_hi, o_split = (sem(n) for n in
                                                      ("o_sq", "o_sum", "o_root", "o_norm", "o_hi", "o_split"))
        gate_act, gate_mul = sem("gate_act"), sem("gate_mul")
        scaled = sem("scaled")
        chunk_in, a_done, a_masked = sem("chunk_in"), sem("a_done"), sem("a_masked")
        tr_done, tr_evac = sem("tr_done"), sem("tr_evac")
        lt_ready, z1_done, z1_ready, t_done, xx_ready, tt_done, xt_ready = (
            sem(n) for n in ("lt_ready", "z1_done", "z1_ready", "t_done", "xx_ready", "tt_done", "xt_ready"))
        rhs_done, rhs_ready, u_done, u_ready = (sem(n) for n in ("rhs_done", "rhs_ready", "u_done", "u_ready"))
        vrow_ready = sem("vrow_ready")
        h_done, h_ready, y_done, y_evac = (sem(n) for n in ("h_done", "h_ready", "y_done", "y_evac"))
        g_done, g_evac = sem("g_done"), sem("g_evac")
        y_mean, y_cent, y_sq, y_var, y_root, y_out, y_hi, y_split = (
            sem(n) for n in ("y_mean", "y_cent", "y_sq", "y_var", "y_root", "y_out", "y_hi", "y_split"))
        mix_act, mix_sum, mix_hi, mix_split = (
            sem(n) for n in ("mix_act", "mix_sum", "mix_hi", "mix_split"))
        ln_acc, ln_mean, ln_cent, ln_sq, ln_pair, ln_var, ln_root, ln_norm = (
            sem(n) for n in ("ln_acc", "ln_mean", "ln_cent", "ln_sq", "ln_pair", "ln_var", "ln_root", "ln_norm"))
        ff_gate, ff_conv, ff_sig, ff_prod, ff_hi, ff_split = (
            sem(n) for n in ("ff_gate", "ff_conv", "ff_sig", "ff_prod", "ff_hi", "ff_split"))
        down_done, x_whole = sem("down_done"), sem("x_whole")
        out_stored, cleared, chunk_clear = sem("out_stored"), sem("cleared"), sem("chunk_clear")
        gate_pe, gate_ac, gate_dve = sem("pe_gate"), sem("act_gate"), sem("dve_gate")

        ident = cst[:, K_ID:K_ID + P]
        ident64 = cst[0:CH, K_ID:K_ID + CH]
        ones = cst[:, K_ONE:K_ONE + P]
        spare = cst[:, K_EPS + 4:K_EPS + 5]
        blk = cst[:, K_BLK:K_BLK + P]

        def over(ap, n):
            return ap.unsqueeze(1).to_broadcast([ap.shape[0], n, ap.shape[1]])

        HALF = (slice(0, T // 2), slice(T // 2, T))
        Z_BANK, T_BANK = (4, 0), (3, 1)
        O_BANKS = ((0, 3), (4, 5))

        C2 = CH // 2

        def quarter(ap, row, col):
            return ap[row:row + C2].rearrange("q (h t) -> q h t", t=CH)[:, :, col:col + C2]

        block = ctx.enter_context(nc.Block())

        @block.sync
        def _(sp):
            xs = x_d.rearrange("(k p) t -> p k t", p=P)
            for s in range(RING):
                sp.dma_start(raw[s][:, :], w_d[0, s]).then_inc(raw_loaded[s], 16)
                if s == 0:
                    for half in range(2):
                        r = slice(4 * half, 4 * half + 4)
                        sp.dma_start(x_sum[:, r, :], xs[:, r, :]).then_inc(x_loaded[half], 16)
            sp.dma_start(cst[:, :], const_d).then_inc(const_loaded, 16)
            with sp.Fori(1, ALL_UNITS // RING) as i:
                group = w_d[bass.ds(i, 1)].rearrange("a s p n -> (a s) p n")
                freed = [sp.snap(3 * i - 2 + s) for s in range(RING)]
                for s in range(RING):
                    sp.wait_ge(lo_ready, freed[s])
                    sp.dma_start(raw[s][:, :], group[s]).then_inc(raw_loaded[s], 16)
            for s in range(2):
                sp.wait_ge(lo_ready, ALL_UNITS - 2 + s)
                sp.dma_start(raw[s][:, :], w_d[ALL_UNITS // RING, s]).then_inc(raw_loaded[s], 16)
            sp.wait_ge(lo_ready, ALL_UNITS + 2)

        @block.gpsimd
        def _(pool):
            def low(s, n, first=False):
                pool.wait_ge(hi_ready, n + 1)
                if not first:
                    pool.wait_ge(unit_done, n - 1)
                nc.gpsimd.tensor_tensor(lo[s][:, :], raw[s][:, :], hi[s][:, :], ALU.subtract).then_inc(lo_ready, 1)

            for s in range(RING):
                low(s, s, True)
            with pool.Fori(1, ALL_UNITS // RING) as i:
                for s in range(RING):
                    low(s, 3 * i + s)
            low(0, ALL_UNITS)
            low(1, ALL_UNITS + 1)

        @block.scalar
        def _(a):
            A = nc.scalar.activation

            def split_x(j, src):
                A(xh[:, j, :], src, ACT.Copy).then_inc(x_hi, 1)

            def split(s, n, turn):
                a.wait_ge(raw_loaded[s], 16 * turn + 16)
                if not isinstance(n, int):
                    a.wait_ge(unit_done, n - 1)
                A(hi[s][:, :], raw[s][:, :], ACT.Copy).then_inc(hi_ready, 1)

            split(0, 0, 0)
            for j in range(KT):
                if j % 4 == 0:
                    a.wait_ge(x_loaded[j // 4], 16)
                split_x(j, x_sum[:, j, :])
            split(1, 1, 0)
            for s, n in ((z_evac, 3), (gate_act, 2), (mix_act, 2), (ff_gate, 2)):
                a.sem_inc(s, n)
            with a.Fori(0, LAYERS) as l:
                u0 = l * UNITS
                t0 = l * (UNITS // RING)

                def unit(k, i=None, each=0):
                    m = k + 2
                    n, turn = u0 + m, t0 + m // RING
                    if i is not None:
                        n, turn = n + i * each, turn + i * (each // RING)
                    split(m % RING, n, turn)
                    a.wait_ge(unit_done, n)

                def gated_wait(s, v):
                    a.wait_ge(s, v)
                    a.sem_inc(gate_ac, 1)

                a.wait_ge(x_split, 16 * l + 8)
                a.dma_start(par[:, :], par_d[bass.ds(l, 1)].rearrange("a p n -> (a p) n")).then_inc(par_loaded, 16)
                for i in range(2):
                    a.dma_start(tab[i][:, :], tab_d[i]).then_inc(tab_loaded[i], 16)

                with a.Fori(0, RH) as h:
                    for part in range(2):
                        unit(U_RET + part, h, 3)
                        scale = 1.0 if part == 0 else float(P) ** -0.5
                        a.wait_ge(ret_in, 12 * l + 3 * h + part + 1)
                        A(tmp[part][0:64, :], ps[64:128, part, :], ACT.Copy, scale=scale)
                        A(tmp[part][64:128, :], ps[0:64, part, :], ACT.Copy, scale=scale).then_inc(ret_evac, 1)
                    unit(U_RET + 2, h, 3)
                    a.wait_ge(ret_in, 12 * l + 3 * h + 3)
                    A(tmp[2][:, :], ps[:, 2, :], ACT.Sigmoid).then_inc(ret_evac, 1)
                a.wait_ge(ret_in, 12 * l + 15)
                for i in range(2):
                    a.dma_start(tab[i][:, :], tab_d[2 + i]).then_inc(tab_loaded[i], 16)
                for k in range(4):
                    unit(U_RETV + k)
                for t in range(4):
                    A(vn[:, t, :], ps[:, 3 + t, :], ACT.Copy).then_inc(v_nat, 1)

                a.wait_ge(cleared, 4 * l + 4)
                a.wait_ge(const_loaded, 16)
                for k in range(3):
                    unit(U_LORA + k)
                    A(zl[:, k, 1:T + 1], ps[:, (U_LORA + k) % RING, :], ACT.Copy).then_inc(z_evac, 1)
                a.wait_ge(z_shifted, 15 * l + 3)
                A(zl[0:64, 0, 1:T + 1], zl[0:64, 0, 1:T + 1], ACT.Tanh).then_inc(lora_act, 1)
                A(zl[:, 1, 1:T + 1], zl[:, 1, 1:T + 1], ACT.Sigmoid).then_inc(lora_act, 1)
                A(zl[0:32, 2, 1:T + 1], zl[0:32, 2, 1:T + 1], ACT.Sigmoid).then_inc(lora_act, 1)
                for p in range(RW_TILES):
                    for k, z in enumerate((zr, zk, zv)):
                        if k == 2:
                            a.wait_ge(o_acc, 16 * l + 4 * p + 4)
                            A(o_ret[:, p, :], ps[:, 5, :], ACT.Copy)
                            if p < 2:
                                a.dma_start(tab[p][:, :], tab_d[4 + p]).then_inc(tab_loaded[p], 16)
                            if p:
                                a.wait_ge(o_norm, 4 * l + p)
                            A(tmp[2][:, :], ps[:, 5, :], ACT.Square).then_inc(o_sq, 1)
                        unit(U_RKV + 3 * p + k)
                        first = CH if z is zv else 1
                        A(z[:, p, first:first + T], ps[:, (U_RKV + k) % RING, :], ACT.Copy).then_inc(z_evac, 1)
                        if k == 2:
                            a.wait_ge(o_sum, 4 * l + p + 1)
                            A(tmp[2][:, :], ps[:, 6, :], ACT.Sqrt, scale=1.0 / P,
                              bias=cst[:, K_EPS + 1:K_EPS + 2]).then_inc(o_root, 1)

                for p in range(4):
                    b = 3 if p % 2 == 0 else 0
                    dsts = (bon[:, p, :], ka_[:, p, :], pd[:, p, 0:T])
                    for k, (dst, c) in enumerate(zip(dsts, (C_W0, C_A0, C_V0))):
                        a.wait_ge(lora_done, 12 * l + 3 * p + k + 1)
                        A(dst, ps[:, (3, 4, 5)[k] if p % 2 == 0 else (6, 7, 0)[k], :], ACT.Sigmoid,
                          bias=par[:, c + p:c + p + 1]).then_inc(lora_evac, 1)
                for p in range(4):
                    a.wait_ge(kk_raw, 4 * l + p + 1)
                    a.wait_ge(scanned, 4 * l + p + 1)
                    A(bon[:, p, :], kn[:, p, :], ACT.Square).then_inc(kk_sq, 1)
                for h in range(RH):
                    a.wait_ge(o_norm, 4 * l + h + 1)
                    A(oh[:, h, :], o_ret[:, h, :], ACT.Copy).then_inc(o_hi, 1)
                for p in range(4):
                    a.wait_ge(v_mixed, 4 * l + p + 1)
                    A(pd[:, p, :].rearrange("q (c j) -> q c j", c=NCH)[:, :, 1:CH + 1],
                      pi[:, p, :].rearrange("q (c j) -> q c j", c=NCH), ACT.Exp, scale=-LOG_DECAY)
                    A(pi[:, p, :], pi[:, p, :], ACT.Exp, scale=LOG_DECAY).then_inc(decay_done, 1)
                for p in range(4):
                    a.wait_ge(kk_sum, 4 * l + p + 1)
                    A(bon[:, p, :], ps[:, 4 + p, :], ACT.Sqrt).then_inc(kk_root, 1)

                with a.Fori(0, 4) as m:
                    for k in range(2):
                        unit(U_GA + k, m, 3)
                        a.wait_ge(gate_mul, 8 * l + 2 * m + k + 1)
                        A(tmp[k][:, :], ps[:, 1 + k, :], ACT.Sigmoid).then_inc(gate_act, 1)
                    unit(U_GA + 2, m, 3)

                def stage(c, b):
                    a.sem_inc(gate_ac, 1)
                    for dst, z, off in (
                            (vc[:, :, CH:2 * CH], zv, CH), (bkc[:, :, 0, :], ka_, 0), (bkc[:, :, 1, :], zk, 1),
                            (arc[b][:, :, 0, :], kn, 0), (arc[b][:, :, 1, :], zr, 1)):
                        if isinstance(c, int):
                            src = z[:, :, off + c * CH:off + (c + 1) * CH]
                        else:
                            src = z[:, :, bass.ds(c * CH + off, CH)]
                        A(dst, src, ACT.Copy).then_inc(chunk_in, 1)

                def by_token(k, b):
                    for i, dst in enumerate((vz[b], bkn[b])):
                        a.wait_ge(tr_done, 2 * (8 * l + k) + i + 1)
                        A(dst[:, :], ps[:, (5, 2)[i], :], ACT.Copy).then_inc(tr_evac, 1)

                def z1_copy(k, level):
                    for half in range(2):
                        a.wait_ge(z1_done, 12 * (8 * l + k) + 2 * level + half + 1)
                        dst, src = z1[:, HALF[half]], ps[0:CH, Z_BANK[half], HALF[half]]
                        if level == 5:
                            dst, src = quarter(dst, C2, 0), quarter(src, C2, 0)
                        A(dst, src, ACT.Copy).then_inc(z1_ready, 1)

                def rhs_copy(k):
                    a.wait_ge(rhs_done, 8 * l + k + 1)
                    A(rhs[0:CH, :], ps[CH:P, 4, :], ACT.Copy).then_inc(rhs_ready, 1)

                def y_copy(c, k):
                    gated_wait(y_done, 8 * l + k + 1)
                    if isinstance(c, int):
                        dst = zr[:, :, 1 + c * CH:1 + (c + 1) * CH]
                    else:
                        dst = zr[:, :, bass.ds(c * CH + 1, CH)]
                    A(dst, ps[:, 6, 0:4 * CH].rearrange("q (p t) -> q p t", p=4), ACT.Copy).then_inc(y_evac, 1)

                a.wait_ge(scaled, 4 * l + 4)
                stage(0, 0)
                by_token(0, 0)
                for level in range(1, 6):
                    z1_copy(0, level)

                def chunk(c, b, k, last=False):
                    if not last:
                        a.wait_ge(tr_done, 2 * (8 * l + k) + 2)
                        if not (isinstance(k, int) and k == 0):
                            a.wait_ge(y_done, 8 * l + k)
                            a.wait_ge(vrow_ready, 8 * l + k)
                        stage(c + 1, 1 - b)
                    rhs_copy(k)
                    if not last:
                        by_token(k + 1, 1 - b)
                    y_copy(c, k)
                    if not last:
                        for level in range(1, 6):
                            z1_copy(k + 1, level)

                chunk(0, 0, 0)
                with a.Fori(0, 3) as i:
                    chunk(2 * i + 1, 1, 2 * i + 1)
                    chunk(2 * i + 2, 0, 2 * i + 2)
                chunk(7, 1, 7, True)

                for p in range(4):
                    a.wait_ge(g_done, 4 * l + p + 1)
                    A(kn[:, p, :], ps[:, p % 2, :], ACT.Copy).then_inc(g_evac, 1)
                for p in range(4):
                    a.wait_ge(y_cent, 4 * l + p + 1)
                    A(tmp[p][:, :], zr[:, p, 1:T + 1], ACT.Square).then_inc(y_sq, 1)
                for g in range(KT):
                    unit(U_GB + g)
                    A(gb[:, g, :], ps[:, 1 + g % 2, :], ACT.Sigmoid).then_inc(mix_act, 1)
                    if g == 0:
                        for p in range(4):
                            a.wait_ge(y_var, 4 * l + p + 1)
                            A(tmp[p][:, :], ps[:, 4 + p, :], ACT.Sqrt, scale=1.0 / CH,
                              bias=cst[:, K_EPS + 2:K_EPS + 3]).then_inc(y_root, 1)
                    if 3 <= g <= 6:
                        a.wait_ge(y_out, 4 * l + g - 2)
                        A(yh[:, g - 3, :], zr[:, g - 3, 1:T + 1], ACT.Copy).then_inc(y_hi, 1)

                for m in range(4):
                    unit(U_GB + KT + m)
                    for k in range(2):
                        a.wait_ge(mix_sum, 8 * l + 2 * m + k + 3)
                        A(mh[:, 2 * m + k, :], tmp[k][:, :], ACT.Copy).then_inc(mix_hi, 1)

                def norm(n, beta):
                    for j in range(KT):
                        a.wait_ge(ln_cent, 8 * n + j + 1)
                        if j >= 4:
                            a.wait_ge(ln_var, 4 * n + j // 2 - 1)
                        A(tmp[j % 4][:, :], x_sum[:, j, :], ACT.Square).then_inc(ln_sq, 1)
                    A(spare, cst[:, K_EPS:K_EPS + 1], ACT.Sqrt)
                    a.wait_ge(ln_var, 4 * n + 4)
                    A(tmp[0][:, :], ps[:, 5, :], ACT.Sqrt, scale=1.0 / D, bias=cst[:, K_EPS:K_EPS + 1])\
                        .then_inc(ln_root, 1)
                    for j in range(KT):
                        a.wait_ge(ln_norm, 8 * n + j + 1)
                        A(xh[:, j, :], x_sum[:, j, :], ACT.Identity, bias=par[:, beta + j:beta + j + 1])\
                            .then_inc(x_hi, 1)

                for j in range(KT):
                    unit(U_OUT + j)
                norm(2 * l, C_L1B)

                def ff_pair(b, u, j, i=None):
                    n = 22 * l + j
                    unit(u, i, 6)
                    a.wait_ge(ff_split, n + 1)
                    A(cg[b][:, 2:T + 2], ps[:, u % RING, :], ACT.Copy)
                    a.sem_inc(gate_ac, 1)
                    if isinstance(j, int):
                        w2, cb = par[:, C_CW + 3 * j + 2:C_CW + 3 * j + 3], par[:, C_CB + j:C_CB + j + 1]
                    else:
                        w2, cb = par[:, bass.ds(C_CW + 2 + 3 * j, 1)], par[:, bass.ds(C_CB + j, 1)]
                    A(cc[b][:, :], ps[:, u % RING, :], ACT.Identity, scale=w2, bias=cb).then_inc(ff_gate, 1)
                    unit(u + 1, i, 6)
                    a.wait_ge(ff_conv, n + 1)
                    A(sg[:, :], cc[b][:, :], ACT.Sigmoid).then_inc(ff_sig, 1)
                    gated_wait(ff_prod, n + 3)
                    dst = ah[:, j, :] if isinstance(j, int) else ah[:, bass.ds(j, 1), :].rearrange("q a t -> q (a t)")
                    A(dst, fa[:, :], ACT.Copy).then_inc(ff_hi, 1)

                with a.Fori(0, 7) as i:
                    for k in range(3):
                        ff_pair(0, U_UP + 2 * k, 3 * i + k, i)
                ff_pair(0, U_UP + 42, 21)

                unit(U_DOWN)
                with a.Fori(0, 6) as i:
                    for k in range(3):
                        unit(U_DOWN + 1 + k, i, 3)
                for k in range(3):
                    unit(U_DOWN + 19 + k)
                norm(2 * l + 1, C_L2B)
            out = out_d.rearrange("(k p) t -> p k t", p=P)
            for j in range(0, KT, 2):
                a.wait_ge(x_whole, j + 2)
                a.dma_start(out[:, j:j + 2, :], x_sum[:, j:j + 2, :]).then_inc(out_stored, 16)
            a.wait_ge(out_stored, 64)

        @block.vector
        def _(v):
            V = nc.vector
            step = Count(dve, 0)
            step.per_layer = 238

            def do(instruction):
                step.inc(instruction)

            def settle():
                v.wait_ge(dve, step.now)

            V.memset(v_first[:, :, :], 0.0)
            for s, n in ((ret_in, 3), (gate_mul, 2), (mix_sum, 2), (mix_split, 2), (ff_prod, 2), (ff_split, 1)):
                v.sem_inc(s, n)
            for j in range(KT):
                v.wait_ge(x_hi, j + 1)
                V.tensor_tensor(xl[:, j, :], x_sum[:, j, :], xh[:, j, :], ALU.subtract).then_inc(x_split, 1)

            with v.Fori(0, LAYERS) as l:
                step.layer(l)
                u0 = l * UNITS

                for i in range(2):
                    v.wait_ge(tab_loaded[i], 48 * l + 16)
                v.wait_ge(x_split, 16 * l + 8)
                v.sem_inc(gate_dve, 1)
                with v.Fori(0, RH) as h:
                    step.enter(h, 4)
                    for part in range(2):
                        dst = qk[:, bass.ds(h + 4 * part, 1), :].rearrange("q a t -> q (a t)")
                        v.wait_ge(ret_evac, 12 * l + 3 * h + part + 1)
                        do(V.scalar_tensor_tensor(out=dst, in0=ps[:, part, :], scalar=float(P) ** (-0.5 * part),
                                                  in1=tab[0][:, :], op0=ALU.mult, op1=ALU.mult))
                        do(V.tensor_tensor(tmp[part][:, :], tmp[part][:, :], tab[1][:, :], ALU.mult))
                        settle()
                        V.tensor_tensor(dst, dst, tmp[part][:, :], ALU.add).then_inc(ret_in, 1)
                    dst = gs[:, bass.ds(h, 1), :].rearrange("q a t -> q (a t)")
                    v.wait_ge(ret_evac, 12 * l + 3 * h + 3)
                    V.tensor_tensor(dst, ps[:, 2, :], tmp[2][:, :], ALU.mult).then_inc(ret_in, 1)
                    step.leave(RH)
                V.memset(zr[:, :, 0:1], 0.0).then_inc(cleared, 1)
                V.memset(zk[:, :, 0:1], 0.0).then_inc(cleared, 1)
                V.memset(zv[:, :, 0:CH], 0.0).then_inc(cleared, 1)
                V.memset(zl[:, :, 0:1], 0.0).then_inc(cleared, 1)
                v.wait_ge(cleared, 4 * l + 4)
                v.wait_ge(par_loaded, 16 * l + 16)
                v.wait_ge(const_loaded, 16)

                def shift(z, first, k, mu):
                    v.wait_ge(z_evac, 15 * l + k + 4)
                    settle_shift(k)
                    do(V.tensor_tensor(tmp[3][:, :], z(first - 1), z(first), ALU.subtract))
                    settle()
                    V.scalar_tensor_tensor(out=z(first), in0=tmp[3][:, :], scalar=mu, in1=z(first), op0=ALU.mult,
                                           op1=ALU.add).then_inc(z_shifted, 1)

                def settle_shift(k):
                    v.wait_ge(z_shifted, 15 * l + k)

                for k in range(3):
                    if k == 0:
                        v.wait_ge(z_evac, 15 * l + 4)
                        do(V.tensor_tensor(tmp[3][:, :], zl[:, 0, 0:T], zl[:, 0, 1:T + 1], ALU.subtract))
                        settle()
                        V.scalar_tensor_tensor(out=zl[:, 0, 1:T + 1], in0=tmp[3][:, :],
                                               scalar=par[:, C_MU:C_MU + 1], in1=zl[:, 0, 1:T + 1], op0=ALU.mult,
                                               op1=ALU.add).then_inc(z_shifted, 1)
                    else:
                        shift(lambda f, k=k: zl[:, k, f:f + T], 1, k, par[:, C_MU + k:C_MU + k + 1])
                def score(n):
                    h, s = n // 4, n % 4
                    w = T - P * s
                    if s == 0:
                        v.wait_ge(tab_loaded[h % 2], 48 * l + 32 + 16 * (h // 2))
                    v.wait_ge(st_done, 16 * l + n + 1)
                    if n >= 2:
                        v.wait_ge(o_acc, 16 * l + n - 1)
                    V.tensor_tensor(tmp[n % 2][:, 0:w], ps[:, 3 + n % 2, 0:w], tab[h % 2][:, 0:w], ALU.mult)\
                        .then_inc(sc_ready, 1)

                def head_out(h):
                    v.wait_ge(o_root, 4 * l + h + 1)
                    do(V.reciprocal(tmp[2][:, :], tmp[2][:, :]))
                    settle()
                    do(V.tensor_tensor(o_ret[:, h, :], o_ret[:, h, :], tmp[2][:, :], ALU.mult))
                    settle()
                    V.tensor_tensor(o_ret[:, h, :], o_ret[:, h, :], gs[:, h, :], ALU.mult).then_inc(o_norm, 1)

                for p in range(RW_TILES):
                    score(4 * p)
                    score(4 * p + 1)
                    if p:
                        head_out(p - 1)
                    for k, z in enumerate((zr, zk, zv)):
                        first = CH if z is zv else 1
                        shift(lambda f, z=z: z[:, p, f:f + T], first, 3 + 3 * p + k,
                              par[:, C_MU + 3 + 3 * p + k:C_MU + 4 + 3 * p + k])
                        if k == 0:
                            score(4 * p + 2)
                            score(4 * p + 3)
                    v.wait_ge(z_shifted, 15 * l + 3 * p + 6)
                    d, vp = tmp[3], zv[:, p, CH:CH + T]
                    do(V.tensor_tensor(d[:, :], v_first[:, p, :], vp, ALU.subtract))
                    settle()
                    do(V.scalar_tensor_tensor(out=v_first[:, p, :], in0=d[:, :], scalar=par[:, C_SEL:C_SEL + 1],
                                              in1=vp, op0=ALU.mult, op1=ALU.add))
                    settle()
                v.wait_ge(z_shifted, 15 * l + 15)

                do(V.tensor_scalar(nka[:, :], par[:, C_KA:C_KA + 4], -1.0, 1.0, ALU.mult, ALU.add))
                for p in range(4):
                    V.tensor_scalar(kn[:, p, :], zk[:, p, 1:T + 1], par[:, C_KK + p:C_KK + p + 1], None, ALU.mult)\
                        .then_inc(kk_raw, 1)
                for p in range(4):
                    v.wait_ge(lora_evac, 12 * l + 3 * p + 3)
                    V.tensor_tensor_scan(pi[:, p, :], cst[:, K_SCAN:K_SCAN + T], bon[:, p, :], 0.0, ALU.mult,
                                         ALU.add).then_inc(scanned, 1)
                    if p == 0:
                        head_out(3)
                for p in range(4):
                    d, vp = tmp[p % 2], zv[:, p, CH:CH + T]
                    do(V.tensor_tensor(d[:, :], v_first[:, p, :], vp, ALU.subtract))
                    settle()
                    do(V.tensor_tensor(d[:, :], d[:, :], pd[:, p, 0:T], ALU.mult))
                    settle()
                    V.tensor_tensor(vp, vp, d[:, :], ALU.add).then_inc(v_mixed, 1)
                    v.wait_ge(v_mixed, 4 * l + p + 1)
                for h in range(RH):
                    v.wait_ge(o_hi, 4 * l + h + 1)
                    V.tensor_tensor(ol[:, h, :], o_ret[:, h, :], oh[:, h, :], ALU.subtract).then_inc(o_split, 1)
                v.wait_ge(decay_done, 4 * l + 4)
                for p in range(4):
                    pv = pd[:, p, :].rearrange("q (c j) -> q c j", c=NCH)
                    do(V.memset(pv[:, :, 0:1], 1.0))
                settle()
                v.wait_ge(kk_root, 4 * l + 4)

                def tile(z, m, off=0, n=T):
                    return z[:, bass.ds(m, 1), off:off + n].rearrange("q a t -> q (a t)")

                def by_chunk(z, m, off, n, step_):
                    return z[:, bass.ds(m, 1), off:off + n].rearrange("q a (c j) -> q (a c) j", j=step_)

                def ma_tile(m, k):
                    return tile(ma, 2 * m + k)

                v.sem_inc(gate_dve, 1)
                with v.Fori(0, 4) as m:
                    step.enter(m, 10)
                    bm, km, kkm, am_, rm = (tile(bon, m), tile(zk, m, 1), tile(kn, m), tile(ka_, m), tile(zr, m, 1))
                    col_m = (lambda c: par[:, bass.ds(c + m, 1)])
                    do(V.tensor_scalar(bm, bm, 1e-12, None, ALU.max))
                    settle()
                    v.sem_inc(gate_dve, 1)
                    do(V.reciprocal(bm, bm))
                    settle()
                    do(V.tensor_tensor(kkm, kkm, bm, ALU.mult))
                    settle()
                    do(V.tensor_scalar(bm, am_, col_m(C_KA), nka[:, bass.ds(m, 1)], ALU.mult, ALU.add))
                    settle()
                    do(V.tensor_tensor(km, km, bm, ALU.mult))
                    settle()
                    V.scalar_tensor_tensor(out=bm, in0=rm, scalar=col_m(C_RK), in1=km, op0=ALU.mult,
                                           op1=ALU.mult).then_inc(bon_in, 1)
                    do(V.tensor_tensor(am_, am_, kkm, ALU.mult))
                    whole = NCH * (CH + 1)
                    pv = by_chunk(pd, m, 0, whole, CH + 1)
                    rc, kc = by_chunk(zr, m, 1, T, CH), by_chunk(kn, m, 0, T, CH)
                    v.wait_ge(bon_in, 4 * l + m + 1)
                    do(V.tensor_tensor(rc, rc, pv[:, :, 1:CH + 1], ALU.mult))
                    do(V.tensor_tensor(km, km, tile(pi, m), ALU.mult))
                    do(V.tensor_copy(pc[:, :, bass.ds(m, 1)], pv[:, :, CH:CH + 1]))
                    settle()
                    do(V.scalar_tensor_tensor(out=kc, in0=kc, scalar=-1.0, in1=pv[:, :, 0:CH], op0=ALU.mult,
                                              op1=ALU.mult))
                    V.tensor_tensor(am_, am_, tile(pi, m), ALU.mult).then_inc(scaled, 1)
                    for k in range(2):
                        v.wait_ge(gate_act, 8 * l + 2 * m + k + 3)
                        v.wait_ge(unit_done, u0 + U_GA + 3 * m + 4)
                        src = ps[:, (0, 3)[k], :]
                        V.tensor_tensor(ma_tile(m, k), src, tmp[k][:, :], ALU.mult).then_inc(gate_mul, 1)
                    v.wait_ge(bon_sum, 4 * l + m + 1)
                    V.tensor_tensor(bm, ps[:, 5, :], tile(zv, m, CH), ALU.mult).then_inc(bon_done, 1)
                    step.leave(4)
                v.wait_ge(gate_mul, 8 * l + 10)
                do(V.memset(hbd[:, :, :], 0.0))
                do(V.memset(hc[:, :, :], 0.0))
                do(V.memset(vc[:, :, 0:CH], 0.0))
                settle()
                v.sem_inc(chunk_clear, 1)
                settle()

                mask = over(cst[:, K_MASK:K_MASK + P], 4)

                def heads(ap, b):
                    return ap

                def level_mask(b, level):
                    return over(cst[0:CH, K_LEV + level * CH:K_LEV + (level + 1) * CH], 8)

                def lt(k, b, level):
                    n = 8 * l + k
                    src = am[b][0:CH, :, :, 0:CH].rearrange("q a h t -> q (a h) t")
                    if level:
                        v.wait_ge(z1_done, 12 * n + 2 * level)
                    dst, mask_ = ltm[0:CH, :].rearrange("q (h t) -> q h t", h=8), level_mask(b, level)
                    if level == 5:
                        dst, src, mask_ = (z[0:C2, :, C2:CH] for z in (dst, src, mask_))
                    V.tensor_tensor(dst, src, mask_, ALU.mult).then_inc(lt_ready, 1)

                def masked(k, b):
                    for par_ in range(2):
                        v.wait_ge(a_done, 2 * (8 * l + k) + par_ + 1)
                        V.tensor_tensor(am[b][:, par_, :, :], ps[:, par_, :].rearrange("q (h t) -> q h t", h=4),
                                        mask, ALU.mult).then_inc(a_masked, 1)
                    v.wait_ge(a_masked, 2 * (8 * l + k) + 2)

                def grow(k, b, level):
                    c8 = 8 * l + k
                    h4 = (lambda ap: ap.rearrange("q (h t) -> q h t", h=4))
                    if level == 0:
                        v.wait_ge(lt_ready, 6 * c8 + 1)
                        for half in HALF:
                            V.tensor_tensor(h4(xt[b][:, half]), h4(ltm[0:CH, half]), over(ident64, 4), ALU.add)\
                                .then_inc(xt_ready, 1)
                        for half in range(2):
                            v.wait_ge(z1_done, 12 * c8 + half + 1)
                            V.tensor_tensor(h4(xx[:, HALF[half]]), h4(ps[0:CH, Z_BANK[half], HALF[half]]),
                                            over(ident64, 4), ALU.add).then_inc(xx_ready, 1)
                        v.wait_ge(xt_ready, 12 * c8 + 2)
                        lt(k, b, 1)
                        return
                    if level < 5:
                        lt(k, b, level + 1)
                        for half in range(2):
                            v.wait_ge(t_done, 8 * c8 + 2 * level - 1 + half)
                            dst, src = xx[:, HALF[half]], ps[0:CH, T_BANK[half], HALF[half]]
                            if level == 4:
                                dst, src = quarter(dst, 0, 0), quarter(src, 0, 0)
                            V.tensor_tensor(dst, src, dst, ALU.add).then_inc(xx_ready, 1)
                    for half in range(2):
                        v.wait_ge(tt_done, 10 * c8 + 2 * level - 1 + half)
                        dst, src = xt[b][:, HALF[half]], ps[CH:P, T_BANK[half], HALF[half]]
                        if level == 5:
                            dst, src = quarter(dst, 0, C2), quarter(src, 0, C2)
                        V.tensor_tensor(dst, src, dst, ALU.add).then_inc(xt_ready, 1)

                def v_rows(k, b):
                    V.tensor_copy(uv[CH:P, :], vz[b][CH:P, :]).then_inc(vrow_ready, 1)

                def u_copy(k):
                    v.wait_ge(u_done, 8 * l + k + 1)
                    V.tensor_copy(uv[0:CH, :], ps[0:CH, 5, :]).then_inc(u_ready, 1)

                def state(c, k):
                    v.wait_ge(h_done, 8 * l + k + 1)
                    v.wait_ge(y_done, 8 * l + k + 1)
                    do(V.tensor_tensor(ht[:, :, :], ps[:, 7, 0:4 * CH].rearrange("q (p i) -> q p i", p=4),
                                       hc[:, :, :], ALU.add))
                    settle()
                    if isinstance(c, int):
                        scale = pc[:, c, :]
                    else:
                        scale = pc[:, bass.ds(c, 1), :].rearrange("q a p -> q (a p)")
                    scale = scale.unsqueeze(2).to_broadcast([P, 4, CH])
                    for half in range(2):
                        r = slice(half * CH, half * CH + CH)
                        do(V.tensor_tensor(hbd[r, :, r], ht[r], scale[r], ALU.mult))
                    V.tensor_tensor(hc[:, :, :], ht[:, :, :], scale, ALU.mult).then_inc(h_ready, 1)
                    v.wait_ge(h_ready, 8 * l + k + 1)
                    settle()

                masked(0, 0)
                lt(0, 0, 0)
                for level in range(6):
                    grow(0, 0, level)
                v.wait_ge(tr_evac, 16 * l + 1)
                v_rows(0, 0)

                def chunk(c, b, k, last=False):
                    nb = 1 - b
                    if not last:
                        masked(k + 1, nb)
                        lt(k + 1, nb, 0)
                    u_copy(k)
                    if not last:
                        grow(k + 1, nb, 0)
                    state(c, k)
                    if not last:
                        grow(k + 1, nb, 1)
                        v.wait_ge(tr_evac, 2 * (8 * l + k + 1) + 1)
                        v_rows(k + 1, nb)
                        for level in range(2, 6):
                            grow(k + 1, nb, level)

                chunk(0, 0, 0)
                v.sem_inc(gate_dve, 1)
                with v.Fori(0, 3) as i:
                    step.enter(i, 6)
                    chunk(2 * i + 1, 1, 2 * i + 1)
                    chunk(2 * i + 2, 0, 2 * i + 2)
                    step.leave(3)
                chunk(7, 1, 7, True)

                v.wait_ge(y_evac, 8 * l + 8)
                for p in range(4):
                    v.wait_ge(y_mean, 4 * l + p + 1)
                    V.scalar_tensor_tensor(out=zr[:, p, 1:T + 1], in0=ps[:, 2 + p % 2, :], scalar=-1.0 / CH,
                                           in1=zr[:, p, 1:T + 1], op0=ALU.mult, op1=ALU.add).then_inc(y_cent, 1)
                for p in range(4):
                    yp = zr[:, p, 1:T + 1]
                    v.wait_ge(y_root, 4 * l + p + 1)
                    do(V.reciprocal(tmp[p][:, :], tmp[p][:, :]))
                    settle()
                    do(V.scalar_tensor_tensor(out=yp, in0=yp, scalar=par[:, C_LXG + p:C_LXG + p + 1],
                                              in1=tmp[p][:, :], op0=ALU.mult, op1=ALU.mult))
                    settle()
                    do(V.scalar_tensor_tensor(out=yp, in0=yp, scalar=par[:, C_LXB + p:C_LXB + p + 1],
                                              in1=bon[:, p, :], op0=ALU.add, op1=ALU.add))
                    settle()
                    v.wait_ge(g_evac, 4 * l + p + 1)
                    V.tensor_tensor(yp, yp, kn[:, p, :], ALU.mult).then_inc(y_out, 1)
                for p in range(4):
                    v.wait_ge(y_hi, 4 * l + p + 1)
                    V.tensor_tensor(yl[:, p, :], zr[:, p, 1:T + 1], yh[:, p, :], ALU.subtract).then_inc(y_split, 1)

                for m in range(4):
                    v.wait_ge(unit_done, u0 + U_GB + KT + m + 2)
                    if m:
                        v.wait_ge(mix_split, 8 * l + 2 * m + 2)
                    for k in range(2):
                        j = 2 * m + k
                        do(V.tensor_tensor(tmp[k][:, :], ps[:, O_BANKS[m % 2][k], :], gb[:, j, :], ALU.mult))
                        settle()
                        V.tensor_tensor(tmp[k][:, :], tmp[k][:, :], ma[:, j, :], ALU.add).then_inc(mix_sum, 1)
                    for k in range(2):
                        j = 2 * m + k
                        v.wait_ge(mix_hi, 8 * l + j + 1)
                        V.tensor_tensor(ml[:, j, :], tmp[k][:, :], mh[:, j, :], ALU.subtract).then_inc(mix_split, 1)

                def carry():
                    for j in range(KT):
                        do(V.tensor_tensor(x_sum[:, j, :], xh[:, j, :].bitcast(F32), xl[:, j, :].bitcast(F32),
                                           ALU.add))
                    settle()

                def residual(j, bank):
                    xs = x_sum[:, j, :]
                    do(V.scalar_tensor_tensor(out=xs, in0=xs, scalar=ALPHA, in1=ps[:, bank, :], op0=ALU.mult,
                                              op1=ALU.add))
                    settle()
                    if j == 1:
                        do(V.tensor_tensor(tmp[0][:, :], x_sum[:, 0, :], xs, ALU.add))
                        settle()
                    elif j > 1:
                        ins = V.tensor_tensor(tmp[0][:, :], tmp[0][:, :], xs, ALU.add)
                        if j == KT - 1:
                            ins.then_inc(ln_acc, 1)
                        else:
                            do(ins)
                            settle()

                def norm(n, gamma, beta):
                    v.wait_ge(ln_mean, n + 1)

                    def pair(i):
                        v.wait_ge(ln_sq, 8 * n + 2 * i + 2)
                        t, u = tmp[2 * i % 4], tmp[2 * i % 4 + 1]
                        V.tensor_tensor(t[:, :], t[:, :], u[:, :], ALU.add).then_inc(ln_pair, 1)

                    for j in range(KT):
                        V.scalar_tensor_tensor(out=x_sum[:, j, :], in0=ps[:, 4, :], scalar=-1.0 / D,
                                               in1=x_sum[:, j, :], op0=ALU.mult, op1=ALU.add).then_inc(ln_cent, 1)
                        if j in (2, 4, 6):
                            pair(j // 2 - 1)
                    pair(3)
                    v.wait_ge(ln_root, n + 1)
                    do(V.reciprocal(tmp[1][:, :], tmp[0][:, :]))
                    settle()
                    v.wait_ge(ln_cent, 8 * n + 8)

                    def low(j):
                        v.wait_ge(x_hi, 8 * n + j + 9)
                        V.scalar_tensor_tensor(out=xl[:, j, :], in0=x_sum[:, j, :],
                                               scalar=par[:, beta + j:beta + j + 1], in1=xh[:, j, :],
                                               op0=ALU.add, op1=ALU.subtract).then_inc(x_split, 1)

                    for j in range(KT):
                        V.scalar_tensor_tensor(out=x_sum[:, j, :], in0=x_sum[:, j, :],
                                               scalar=par[:, gamma + j:gamma + j + 1], in1=tmp[1][:, :],
                                               op0=ALU.mult, op1=ALU.mult).then_inc(ln_norm, 1)
                        if j >= 2:
                            low(j - 2)
                    low(KT - 2)
                    low(KT - 1)

                v.wait_ge(mix_split, 8 * l + 10)
                carry()
                for j in range(KT):
                    v.wait_ge(unit_done, u0 + U_OUT + j + 2)
                    residual(j, (j + 6) % 8)
                norm(2 * l, C_L1G, C_L1B)

                v.wait_ge(x_split, 16 * l + 16)
                do(V.memset(cg[0][:, 0:2], 0.0))
                settle()

                def ff_pair(b, u, j, i=None):
                    n = 22 * l + j
                    w = [par[:, C_CW + 3 * j + t:C_CW + 3 * j + t + 1] if isinstance(j, int)
                         else par[:, bass.ds(C_CW + 3 * j + t, 1)] for t in range(2)]
                    v.wait_ge(ff_gate, n + 3)
                    for t in (1, 0):
                        ins = V.scalar_tensor_tensor(out=cc[b][:, :], in0=cg[b][:, t:t + T], scalar=w[t],
                                                     in1=cc[b][:, :], op0=ALU.mult, op1=ALU.add)
                        if t:
                            do(ins)
                            settle()
                        else:
                            ins.then_inc(ff_conv, 1)
                    v.wait_ge(ff_sig, n + 1)
                    do(V.tensor_tensor(cc[b][:, :], cc[b][:, :], sg[:, :], ALU.mult))
                    settle()
                    up = u0 + u + 3 if i is None else u0 + u + 3 + 6 * i
                    v.wait_ge(unit_done, up)
                    V.tensor_tensor(fa[:, :], ps[:, (u + 1) % RING, :], cc[b][:, :], ALU.mult).then_inc(ff_prod, 1)
                    v.wait_ge(ff_hi, n + 1)
                    pick = (lambda z: z[:, j, :] if isinstance(j, int)
                            else z[:, bass.ds(j, 1), :].rearrange("q a t -> q (a t)"))
                    V.tensor_tensor(pick(al), fa[:, :], pick(ah), ALU.subtract).then_inc(ff_split, 1)

                v.sem_inc(gate_dve, 1)
                with v.Fori(0, 7) as i:
                    step.enter(i, 6)
                    for k in range(3):
                        ff_pair(0, U_UP + 2 * k, 3 * i + k, i)
                    step.leave(7)
                ff_pair(0, U_UP + 42, 21)
                v.wait_ge(ff_split, 22 * l + 23)

                carry()
                for j in range(KT):
                    if j < KT - 1:
                        v.wait_ge(down_done, 7 * l + j + 1)
                    else:
                        v.wait_ge(unit_done, u0 + UNITS + 1)
                    residual(j, j)
                norm(2 * l + 1, C_L2G, C_L2B)
                step.end()
            v.wait_ge(x_split, 16 * LAYERS + 8)
            for j in range(KT):
                V.tensor_tensor(x_sum[:, j, :], xh[:, j, :].bitcast(F32), xl[:, j, :].bitcast(F32), ALU.add)\
                    .then_inc(x_whole, 1)

        @block.tensor
        def _(pe):
            MM = nc.tensor.matmul

            def split_product(out, w, x, k, start, stop, last=None):
                (wh, wl), (xh_, xl_) = w, x
                MM(out, wh, xh_, start=start, stop=False)
                MM(out, wl, xh_, start=False, stop=False)
                ins = MM(out, wh, xl_, start=False, stop=stop)
                if last is not None:
                    ins.then_inc(last, 1)

            pe.sem_inc(unit_done, 1)
            with pe.Fori(0, LAYERS) as l:
                u0 = l * UNITS

                def unit_ready(k, i=None, each=0):
                    n = u0 + k + 1
                    pe.wait_ge(lo_ready, n if i is None else n + i * each)

                def dense(k, bank, i=None, each=0, x=None, x_steps=None, x_ready=x_split):
                    unit_ready(k, i, each)
                    s = k % RING
                    for t in range(KT):
                        if x_steps is not None:
                            pe.wait_ge(x_ready, x_steps + t + 1)
                        w = [z[:, t * P:(t + 1) * P] for z in (hi[s], lo[s])]
                        split_product(ps[:, bank, :], w, [z[:, t, :] for z in (x or (xh, xl))], t, t == 0,
                                      t == KT - 1, unit_done if t == KT - 1 else None)

                def half_dense(k, i, each, x, banks):
                    unit_ready(k, i, each)
                    s = k % RING
                    for n in range(2):
                        for t in range(4):
                            w = [z[:, (4 * n + t) * P:(4 * n + t + 1) * P] for z in (hi[s], lo[s])]
                            split_product(ps[:, banks[n], :], w, [z[:, t, :] for z in x], t, t == 0, t == 3,
                                          unit_done if n == 1 and t == 3 else None)

                with pe.Fori(0, RH) as h:
                    for k in range(3):
                        pe.wait_ge(ret_in, 12 * l + 3 * h + k + 1)
                        dense(U_RET + k, k, h, 3, x_steps=16 * l if k == 0 else None)
                for k in range(4):
                    unit_ready(U_RETV + k)
                    s = (U_RETV + k) % RING
                    for t in range(4):
                        for kk in range(2):
                            kt = 2 * k + kk
                            last = t == 3 and kk == 1
                            tok = slice(t * P, (t + 1) * P)
                            wc = slice(kk * 512, kk * 512 + 512)
                            out = ps[:, 3 + t, :]
                            MM(out, xh[:, kt, tok], hi[s][:, wc], start=kt == 0, stop=False)
                            MM(out, xh[:, kt, tok], lo[s][:, wc], start=False, stop=False)
                            ins = MM(out, xl[:, kt, tok], hi[s][:, wc], start=False, stop=kt == KT - 1)
                            if last:
                                ins.then_inc(unit_done, 1)

                pe.wait_ge(const_loaded, 16)
                pe.wait_ge(ret_in, 12 * l + 15)
                for k in range(3):
                    dense(U_LORA + k, (U_LORA + k) % RING)
                def scores(n):
                    h, s = n // 4, n % 4
                    if n < 2:
                        pe.wait_ge(v_nat, 4 * l + 4)
                    else:
                        pe.wait_ge(sc_ready, 16 * l + n - 1)
                    MM(ps[:, 3 + n % 2, 0:T - P * s], qk[:, RH + h, s * P:(s + 1) * P], qk[:, h, s * P:T],
                       start=True, stop=True).then_inc(st_done, 1)

                def output(n):
                    h, s = n // 4, n % 4
                    pe.wait_ge(sc_ready, 16 * l + n + 1)
                    if s == 0 and h:
                        pe.wait_ge(o_sq, 4 * l + h)
                    MM(ps[:, 5, s * P:T], vn[:, s, h * P:(h + 1) * P], tmp[n % 2][:, 0:T - P * s],
                       start=s == 0, stop=s == 3, skip_group_check=True).then_inc(o_acc, 1)

                for p in range(RW_TILES):
                    scores(4 * p)
                    scores(4 * p + 1)
                    for k in range(3):
                        pe.wait_ge(z_evac, 15 * l + 3 * p + k + 4)
                        dense(U_RKV + 3 * p + k, (U_RKV + k) % RING)
                        if k < 2:
                            output(4 * p + 2 * k)
                            if k == 0:
                                scores(4 * p + 2)
                            output(4 * p + 2 * k + 1)
                            if k == 0:
                                scores(4 * p + 3)
                    pe.wait_ge(o_sq, 4 * l + p + 1)
                    if p:
                        pe.wait_ge(o_root, 4 * l + p)
                    MM(ps[:, 6, :], ones, tmp[2][:, :], start=True, stop=True).then_inc(o_sum, 1)

                pe.wait_ge(par_loaded, 16 * l + 16)
                pe.wait_ge(lora_act, 3 * l + 3)
                for p in range(4):
                    c = slice(p * P, (p + 1) * P)
                    banks = (3, 4, 5) if p % 2 == 0 else (6, 7, 0)
                    if p == 1:
                        pe.wait_ge(z_evac, 15 * l + 18)
                        pe.wait_ge(o_root, 4 * l + 4)
                    if p >= 2:
                        pe.wait_ge(lora_evac, 12 * l + 3 * p - 3)
                    MM(ps[:, banks[0], :], par[0:64, C_LW:C_LW + T][:, c], zl[0:64, 0, 1:T + 1], start=True,
                       stop=True).then_inc(lora_done, 1)
                    MM(ps[:, banks[1], :], par[64:128, C_LW:C_LW + T][:, c], zl[64:128, 0, 1:T + 1], start=True,
                       stop=True).then_inc(lora_done, 1)
                    MM(ps[:, banks[2], :], par[:, C_LV:C_LV + T][:, c], zl[:, 2, 1:T + 1], start=True,
                       stop=True).then_inc(lora_done, 1)
                pe.wait_ge(lora_evac, 12 * l + 12)
                for p in range(4):
                    pe.wait_ge(kk_sq, 4 * l + p + 1)
                    MM(ps[:, 4 + p, :], blk, bon[:, p, :], start=True, stop=True).then_inc(kk_sum, 1)

                with pe.Fori(0, 4) as m:
                    for k in range(2):
                        pe.wait_ge(gate_act, 8 * l + 2 * m + k + 1)
                        dense(U_GA + k, 1 + k, m, 3)
                    pe.wait_ge(gate_mul, 8 * l + 2 * m + 2)
                    pe.wait_ge(o_split, 4 * l + 4)
                    half_dense(U_GA + 2, m, 3, (oh, ol), (0, 3))
                    pe.wait_ge(bon_in, 4 * l + m + 1)
                    MM(ps[:, 5, :], blk, bon[:, bass.ds(m, 1), :].rearrange("q a t -> q (a t)"), start=True,
                       stop=True).then_inc(bon_sum, 1)

                def products(k, b):
                    n = 8 * l + k
                    for i in range(2):
                        pe.wait_ge(chunk_in, 5 * n + (1, 3)[i])
                        for p in range(4):
                            src = bkc[:, p, :, :].rearrange("q a t -> q (a t)") if i else vc[:, p, :]
                            ins = nc.tensor.transpose(ps[:, (5, 2)[i], p * P:(p + 1) * P], src, ident)
                        ins.then_inc(tr_done, 1)
                    if not (isinstance(k, int) and k == 0):
                        pe.wait_ge(xt_ready, 12 * n)
                    pe.wait_ge(chunk_in, 5 * n + 5)
                    for par_ in range(2):
                        r = slice(par_ * CH, par_ * CH + CH)
                        for p in range(4):
                            ins = MM(ps[:, par_, p * P:(p + 1) * P], bkc[r, p, :, :].rearrange("q a t -> q (a t)"),
                                     arc[b][r, p, :, :].rearrange("q a t -> q (a t)"), start=True, stop=True)
                        ins.then_inc(a_done, 1)

                def wait64(s, value):
                    pe.wait_ge(s, value)
                    pe.sem_inc(gate_pe, 1)

                H8 = [(h % 2) * 4 + h // 2 for h in range(8)]

                def z1_mm(k, b, level):
                    n = 8 * l + k
                    wait64(lt_ready, 6 * n + level + 1)
                    for half in range(2):
                        if level:
                            wait64(xx_ready, 10 * n + 2 * level - 1 + half)
                        for h in range(4 * half, 4 * half + 4):
                            c = slice(h * CH, (h + 1) * CH)
                            out = ps[0:CH, Z_BANK[half], c]
                            if level == 0:
                                ins = nc.tensor.transpose(out, ltm[0:CH, c], ident64)
                            elif level == 5:
                                w, x = slice(h * CH + C2, (h + 1) * CH), slice(h * CH, h * CH + C2)
                                ins = MM(ps[C2:CH, Z_BANK[half], x], ltm[0:C2, w], xx[0:C2, x], start=True, stop=True)
                            else:
                                ins = MM(out, ltm[0:CH, c], xx[:, c], start=True, stop=True)
                        ins.then_inc(z1_done, 1)

                def t_mm(k, b, level):
                    n = 8 * l + k
                    for half in range(2):
                        pe.wait_ge(xt_ready, 12 * n + 2 * level - 1 + half)
                        wait64(z1_ready, 10 * n + 2 * level - 1 + half)
                        if level < 5:
                            for h in range(4 * half, 4 * half + 4):
                                r, c = slice(0, CH), slice(h * CH, (h + 1) * CH)
                                if level == 4:
                                    r, c = slice(0, C2), slice(h * CH, h * CH + C2)
                                ins = MM(ps[r, T_BANK[half], c], xt[b][r, c], z1[r, c], start=True, stop=True)
                            ins.then_inc(t_done, 1)
                    for half in range(2):
                        for h in range(4 * half, 4 * half + 4):
                            c, r = slice(h * CH, (h + 1) * CH), slice(0, CH)
                            out = ps[CH:P, T_BANK[half], c]
                            if level == 5:
                                c, r = slice(h * CH, h * CH + C2), slice(C2, CH)
                                out = ps[CH:CH + C2, T_BANK[half], h * CH + C2:(h + 1) * CH]
                                ins = MM(out, z1[r, c], xt[b][r, h * CH + C2:(h + 1) * CH], start=True, stop=True)
                            else:
                                ins = MM(out, z1[r, c], xt[b][r, c], start=True, stop=True)
                        ins.then_inc(tt_done, 1)

                def am_of(b, h):
                    return am[b][:, h % 2, h // 2, :]

                def col(h):
                    return slice(H8[h] * CH, (H8[h] + 1) * CH)

                def s1(k, b):
                    n = 8 * l + k
                    first = isinstance(k, int) and k == 0
                    if not first:
                        pe.wait_ge(h_ready, n)
                        pe.wait_ge(y_evac, n)
                        pe.wait_ge(rhs_ready, n)
                    pe.wait_ge(a_masked, 2 * n + 2)
                    pe.wait_ge(tr_evac, 2 * n + 2)
                    for h in range(8):
                        MM(ps[CH:P, 4, col(h)], arc[b][:, h // 2, 0, :], hbd[:, h // 2, (h % 2) * CH:(h % 2) * CH + CH],
                           start=True, stop=False)
                        ins = MM(ps[CH:P, 4, col(h)], am_of(b, h)[:, 0:CH], vz[b][:, h * CH:(h + 1) * CH],
                                 start=False, stop=True)
                    ins.then_inc(rhs_done, 1)

                def s2(k, b, last):
                    n = 8 * l + k
                    if not last:
                        pe.wait_ge(tr_evac, 2 * n + 3)
                    pe.wait_ge(xt_ready, 12 * n + 12)
                    wait64(rhs_ready, n + 1)
                    for h in range(8):
                        ins = MM(ps[0:CH, 5, h * CH:(h + 1) * CH], xt[b][:, col(h)], rhs[0:CH, col(h)], start=True,
                                 stop=True)
                    ins.then_inc(u_done, 1)

                def s34(k, b):
                    n = 8 * l + k
                    pe.wait_ge(u_ready, n + 1)
                    pe.wait_ge(vrow_ready, n + 1)
                    for h in range(8):
                        c = slice(h * CH, (h + 1) * CH)
                        r = slice((h % 2) * CH, (h % 2) * CH + CH)
                        ins = MM(ps[r, 7, (h // 2) * CH:(h // 2 + 1) * CH], bkn[b][:, c], uv[:, c], start=True,
                                 stop=True)
                    ins.then_inc(h_done, 1)
                    for p in range(4):
                        out = ps[:, 6, p * CH:(p + 1) * CH]
                        MM(out, hbd[:, p, :], arc[b][:, p, 1, :], start=True, stop=False, skip_group_check=True)
                        for e in range(2):
                            h = 2 * p + e
                            ins = MM(out[e * CH:(e + 1) * CH], uv[:, h * CH:(h + 1) * CH], am_of(b, h)[:, CH:P],
                                     start=False, stop=True, skip_group_check=True)
                    ins.then_inc(y_done, 1)

                pe.wait_ge(chunk_clear, l + 1)
                products(0, 0)
                for level in range(6):
                    z1_mm(0, 0, level)
                    if 0 < level < 5:
                        t_mm(0, 0, level)

                def chunk(k, b, last=False):
                    nb = 1 - b
                    s1(k, b)
                    t_mm(k, b, 5)
                    if not last:
                        products(k + 1, nb)
                    s2(k, b, last)
                    if not last:
                        z1_mm(k + 1, nb, 0)
                    s34(k, b)
                    if not last:
                        for level in range(1, 6):
                            z1_mm(k + 1, nb, level)
                            if level < 5:
                                t_mm(k + 1, nb, level)

                chunk(0, 0)
                pe.sem_inc(gate_pe, 1)
                with pe.Fori(0, 3) as i:
                    chunk(2 * i + 1, 1)
                    chunk(2 * i + 2, 0)
                chunk(7, 1, True)

                for p in range(4):
                    c = slice(p * P, (p + 1) * P)
                    if p >= 2:
                        pe.wait_ge(g_evac, 4 * l + p - 1)
                    MM(ps[:, p % 2, :], par[:, C_LG:C_LG + T][:, c], zl[:, 1, 1:T + 1], start=True, stop=False)
                    MM(ps[:, p % 2, :], par[:, C_LG2:C_LG2 + T][:, c], zl[:, 2, 1:T + 1], start=False, stop=True)\
                        .then_inc(g_done, 1)
                pe.wait_ge(y_evac, 8 * l + 8)
                for p in range(4):
                    if p >= 2:
                        pe.wait_ge(y_cent, 4 * l + p - 1)
                    MM(ps[:, 2 + p % 2, :], blk, zr[:, p, 1:T + 1], start=True, stop=True).then_inc(y_mean, 1)
                pe.wait_ge(g_evac, 4 * l + 4)
                for g in range(KT):
                    pe.wait_ge(mix_act, 8 * l + g + 1)
                    if g == 1:
                        pe.wait_ge(y_cent, 4 * l + 4)
                    dense(U_GB + g, 1 + g % 2)
                    if g == 0:
                        for p in range(4):
                            pe.wait_ge(y_sq, 4 * l + p + 1)
                            if p == 3:
                                pe.wait_ge(h_ready, 8 * l + 8)
                            MM(ps[:, 4 + p, :], blk, tmp[p][:, :], start=True, stop=True).then_inc(y_var, 1)
                pe.wait_ge(y_split, 4 * l + 4)
                for m in range(4):
                    if m >= 2:
                        pe.wait_ge(mix_sum, 8 * l + 2 * m)
                    half_dense(U_GB + KT + m, None, 0, (yh, yl), O_BANKS[m % 2])

                for j in range(KT):
                    dense(U_OUT + j, (j + 6) % 8, x=(mh, ml), x_steps=8 * l + 2 if j == 0 else None,
                          x_ready=mix_split)

                def norm(n):
                    pe.wait_ge(ln_acc, n + 1)
                    MM(ps[:, 4, :], ones, tmp[0][:, :], start=True, stop=True).then_inc(ln_mean, 1)
                    for i in range(4):
                        pe.wait_ge(ln_pair, 4 * n + i + 1)
                        MM(ps[:, 5, :], ones, tmp[2 * i % 4][:, :], start=i == 0, stop=i == 3).then_inc(ln_var, 1)

                norm(2 * l)

                def bank_free(k, i):
                    if k % 2:
                        pe.wait_ge(ff_gate, 22 * l + 3 * i + k // 2 + 2)
                    else:
                        pe.wait_ge(ff_prod, 22 * l + 3 * i + k // 2 + 1)

                with pe.Fori(0, 7) as i:
                    for k in range(6):
                        bank_free(k, i)
                        dense(U_UP + k, (U_UP + k) % RING, i, 6, x_steps=16 * l + 8 if k == 0 else None)
                for k in range(2):
                    bank_free(k, 7)
                    dense(U_UP + 42 + k, k)
                def down(u, k, start, stop, i=None):
                    unit_ready(u, i, 3)
                    s = u % RING
                    pick = (lambda z: z[:, k, :] if isinstance(k, int)
                            else z[:, bass.ds(k, 1), :].rearrange("q a t -> q (a t)"))
                    for n in (*range(2, 8), 0, 1):
                        if start and n == 0:
                            pe.wait_ge(ff_prod, 22 * l + 24)
                        w = [z[:, n * P:(n + 1) * P] for z in (hi[s], lo[s])]
                        split_product(ps[:, n, :], w, (pick(ah), pick(al)), None, start, stop,
                                      unit_done if n == 1 else None)

                pe.wait_ge(ff_split, 22 * l + 22)
                down(U_DOWN, 0, True, False)
                pe.sem_inc(gate_pe, 1)
                with pe.Fori(0, 6) as i:
                    for k in range(3):
                        down(U_DOWN + 1 + k, 3 * i + k + 1, False, False, i)
                pe.wait_ge(ff_split, 22 * l + 23)
                for n, k in [(n, k) for k in range(3) for n in range(4)] + [(n, k) for n in range(4, 8)
                                                                          for k in range(3)]:
                    u = U_DOWN + 19 + k
                    if n == 0:
                        unit_ready(u)
                    w = [z[:, n * P:(n + 1) * P] for z in (hi[u % RING], lo[u % RING])]
                    done = unit_done if n == 7 else down_done if k == 2 else None
                    split_product(ps[:, n, :], w, (ah[:, 19 + k, :], al[:, 19 + k, :]), None, False, k == 2, done)
                norm(2 * l + 1)


def _layout(inputs):
    import numpy as np
    f = {k: np.asarray(v) for k, v in inputs.items()}
    zero = np.float32(0)

    def tiles(w, cols):
        sub = w[:, cols]
        k = sub.shape[0] // P
        return sub.reshape(k, P, P).transpose(1, 0, 2).reshape(P, k * P)

    w = np.zeros((ALL_UNITS // RING + 1, RING, P, 8 * P), np.float32)
    flat = w.reshape(-1, P, 8 * P)
    par = np.zeros((LAYERS, P, NPAR), np.float32)
    for l in range(LAYERS):
        wi = f["w_in"][l]
        rw = 2048
        order = []
        for h in range(RH):
            order += [h * P, 512 + h * P, 1536 + h * P]
        units = [tiles(wi, slice(c, c + P)) for c in order]
        wv = wi[:, 1024:1536].reshape(4, 2, P, 512)
        units += [wv[k].transpose(1, 0, 2).reshape(P, 8 * P) for k in range(4)]
        last = np.zeros((D, P), np.float32)
        last[:, 0:32] = wi[:, 3840:3872]
        if l:
            last[:, 32:64] = f["w_vres_in"][l - 1]
        units += [tiles(wi, slice(3584, 3712)), tiles(wi, slice(3712, 3840)), tiles(last, slice(0, P))]
        for p in range(4):
            units += [tiles(wi, slice(rw + q * 512 + p * P, rw + q * 512 + (p + 1) * P)) for q in range(3)]
        gate_a, gate_b = ([tiles(wi, slice(first + j * P, first + (j + 1) * P)) for j in range(KT)]
                          for first in (3872, 4896))
        ret_o, rwkv_o = ([np.concatenate([tiles(wo, slice((2 * m + k) * P, (2 * m + k + 1) * P)) for k in range(2)],
                                         axis=1) for m in range(4)] for wo in (f["w_ret_o"][l], f["w_rwkv_o"][l]))
        for m in range(4):
            units += gate_a[2 * m:2 * m + 2] + [ret_o[m]]
        units += gate_b + rwkv_o
        units += [tiles(f["w_out"][l], slice(j * P, (j + 1) * P)) for j in range(KT)]
        for j in range(FT):
            units += [tiles(f["w_up"][l], slice(j * P, (j + 1) * P)),
                      tiles(f["w_up"][l], slice(FF + j * P, FF + (j + 1) * P))]
        units += [f["w_down"][l][k * P:(k + 1) * P] for k in range(FT)]
        assert len(units) == UNITS
        for k, u in enumerate(units):
            flat[l * UNITS + k] = u

        def put(c, a):
            n = a.size // P
            par[l, :, c:c + n] = a.reshape(n, P).T

        mu = f["mu_shift"][l]
        m3 = np.zeros(P, np.float32)
        m3[0:32] = mu[1792:1824]
        if l:
            m3[32:64] = f["mu_vres"][l - 1]
        put(C_MU, np.concatenate([mu[1536:1664], mu[1664:1792], m3]))
        for p in range(4):
            for q in range(3):
                put(C_MU + 3 + 3 * p + q, mu[q * 512 + p * P:q * 512 + (p + 1) * P])
        put(C_W0, f["w0"][l]); put(C_A0, f["a0"][l])
        put(C_KK, f["k_k"][l]); put(C_KA, f["k_a"][l]); put(C_RK, f["r_k"][l].reshape(-1))
        put(C_LXG, f["lnx_g"][l]); put(C_LXB, f["lnx_b"][l])
        put(C_L1G, f["ln1_g"][l]); put(C_L1B, f["ln1_b"][l]); put(C_L2G, f["ln2_g"][l]); put(C_L2B, f["ln2_b"][l])
        par[l, :, C_CW:C_CW + 3 * FT] = f["conv_w"][l].reshape(3, FT, P).transpose(2, 1, 0).reshape(P, 3 * FT)
        put(C_CB, f["conv_b"][l])
        par[l, 0:64, C_LW:C_LW + T] = f["w2"][l]
        par[l, 64:128, C_LW:C_LW + T] = f["a2"][l]
        par[l, :, C_LG:C_LG + T] = f["g2"][l][0:128]
        par[l, 0:32, C_LG2:C_LG2 + T] = f["g2"][l][128:160]
        if l:
            put(C_V0, f["v0"][l - 1])
            par[l, 32:64, C_LV:C_LV + T] = f["v2"][l - 1]
            par[l, :, C_SEL] = 1.0
    return w, par


def _constants():
    import numpy as np
    cst = np.zeros((P, NCONST), np.float32)
    i = np.arange(P)
    cst[:, K_ID:K_ID + P] = np.eye(P)
    cst[:, K_ONE:K_ONE + P] = 1.0
    cst[:, K_BLK:K_BLK + P] = i[:, None] // CH == i[None, :] // CH
    s, t = i[:, None] % CH, i[None, :] % CH
    cst[:, K_MASK:K_MASK + P] = np.where(i[None, :] < CH, s < t, s <= t)
    e = np.arange(CH)
    for level in range(6):
        m = 1 << level
        same = e[:, None] // (2 * m) == e[None, :] // (2 * m)
        low = (e[:, None] // m % 2 == 0) & (e[None, :] // m % 2 == 1)
        cst[0:CH, K_LEV + level * CH:K_LEV + (level + 1) * CH] = same & low
    cst[:, K_SCAN:K_SCAN + T] = (np.arange(T) % CH != 0)[None, :]
    cst[:, K_EPS], cst[:, K_EPS + 1], cst[:, K_EPS + 2] = LN_EPS, RET_EPS, LNX_EPS
    tab = np.zeros((2 + RH, P, T), np.float32)
    half = P // 2
    freq = np.float32(10000.0) ** (-np.arange(half, dtype=np.float32) / np.float32(half))
    ang = (np.arange(T, dtype=np.float32)[None, :] * freq.astype(np.float32)[:, None]).astype(np.float32)
    tab[0] = np.concatenate([np.cos(ang), np.cos(ang)])
    tab[1] = np.concatenate([-np.sin(ang), np.sin(ang)])
    x = np.arange(T)
    for h in range(RH):
        g = 1.0 - 2.0 ** (-5.0 - h)
        d = x[None, :] - i[:, None]
        seen = x[None, :] // CH >= i[:, None] // CH
        tab[2 + h] = np.where(seen, g ** np.abs(d).astype(np.float64), 0.0)
    return cst, tab


def kernel(**inputs):
    import numpy as np
    import concourse.bacc as bacc
    from concourse.bass_utils import run_bass_kernel_spmd

    nc = bacc.Bacc("TRN2", target_bir_lowering=False, num_devices=1)
    w, par = _layout(inputs)
    cst, tab = _constants()
    arrays = {"x_t": np.ascontiguousarray(np.asarray(inputs["x"])[0].T), "weights": w, "params": par,
              "constants": cst, "tables": tab}
    args = [nc.dram_tensor(n, a.shape, F32, kind="ExternalInput").ap() for n, a in arrays.items()]
    args.append(nc.dram_tensor("out_t", (D, T), F32, kind="ExternalOutput").ap())
    build(nc, *args)
    r = run_bass_kernel_spmd(nc, [arrays], core_ids=[0])
    return np.ascontiguousarray(r.results[0]["out_t"].T)[None]
```
